# Optimizing a Trainium2 kernel written in Bass

```python
import jax, jax.numpy as jnp
from jax import lax
import numpy as np

D_MODEL = 1024
BATCH = 1
SEQ = 512
DEPTH = 4

CHUNK = 64
N_MIXERS = 3
CONV_A_WIDTH = 31
CONV_C_WIDTH = 3
SGU_BLOCK = 128
SGU_HEADS = 8
SGU_WIDTH = 2 * D_MODEL
SGU_GROUP = SGU_WIDTH // SGU_HEADS
D_FF = -(-8 * D_MODEL // (3 * 256)) * 256
D_PLE = 256
ALPHA = (2 * DEPTH) ** 0.25
BETA = (8 * DEPTH) ** -0.25
LN_EPS = 1e-5
N_A = (DEPTH + 2) // 3
N_B = (DEPTH + 1) // 3
N_C = DEPTH // 3

kernel_name = "interleaved_conv_sgu_shortconv_deepnorm_trunk"

def layer_norm(x, g, b):
    xf = x.astype(jnp.float32)
    mu = jnp.mean(xf, axis=-1, keepdims=True)
    xc = xf - mu
    var = jnp.mean(xc * xc, axis=-1, keepdims=True)
    y = xc * lax.rsqrt(var + LN_EPS) * g.astype(jnp.float32) + b.astype(jnp.float32)
    return y.astype(x.dtype)

def rms_norm(x, g):
    xf = x.astype(jnp.float32)
    y = xf * lax.rsqrt(jnp.mean(xf * xf, axis=-1, keepdims=True) + LN_EPS) * g.astype(jnp.float32)
    return y.astype(x.dtype)

def causal_depthwise_conv(x, w):
    k, c = w.shape
    return lax.conv_general_dilated(
        x, w[:, None, :].astype(x.dtype), window_strides=(1,), padding=[(k - 1, 0)],
        dimension_numbers=("NWC", "WIO", "NWC"), feature_group_count=c)

def mixer_conformer_conv(x, w_pw1, b_pw1, w_dw, b_dw, ln_g, ln_b, w_pw2):
    h = x @ w_pw1 + b_pw1
    a, g = jnp.split(h, 2, axis=-1)
    h = a * jax.nn.sigmoid(g)
    h = causal_depthwise_conv(h, w_dw) + b_dw
    h = jax.nn.silu(layer_norm(h, ln_g, ln_b))
    return h @ w_pw2

def mixer_sgu(x, w_in, b_in, ln_g, ln_b, w_s, b_s, w_out):
    bsz, seq, _ = x.shape
    z = jax.nn.gelu(x @ w_in + b_in)
    u, v = jnp.split(z, 2, axis=-1)
    v = layer_norm(v, ln_g, ln_b)
    v = v.reshape(bsz, seq // SGU_BLOCK, SGU_BLOCK, SGU_HEADS, SGU_GROUP)
    pos = jnp.arange(SGU_BLOCK) // CHUNK
    mask = pos[:, None] >= pos[None, :]
    w_m = jnp.where(mask[None], w_s, jnp.zeros_like(w_s))
    f = jnp.einsum("hts,bnshg->bnthg", w_m, v) + jnp.transpose(b_s)[None, None, :, :, None]
    return (u * f.reshape(bsz, seq, SGU_WIDTH)) @ w_out

def mixer_short_conv(x, w_in, w_conv, w_out):
    bg, cg, h = jnp.split(x @ w_in, 3, axis=-1)
    y = causal_depthwise_conv(cg * h, w_conv)
    return (bg * y) @ w_out

def swiglu(x, w_gate, w_up, w_down):
    return (jax.nn.silu(x @ w_gate) * (x @ w_up)) @ w_down

def setup_inputs(seed: int = 0) -> dict:
    key = jax.random.key(seed)
    ks = jax.random.split(key, 32)
    f32 = jnp.float32

    def nrm(k, shape, scale):
        return jax.random.normal(k, shape, f32) * scale

    D, E = D_MODEL, SGU_WIDTH
    return {
        "x": nrm(ks[0], (BATCH, SEQ, D), 1.0),
        "p": nrm(ks[1], (DEPTH, BATCH, SEQ, D_PLE), 1.0),
        "a_w_pw1": nrm(ks[2], (N_A, D, 2 * D), D ** -0.5),
        "a_b_pw1": nrm(ks[3], (N_A, 2 * D), 0.02),
        "a_w_dw": nrm(ks[4], (N_A, CONV_A_WIDTH, D), CONV_A_WIDTH ** -0.5),
        "a_b_dw": nrm(ks[5], (N_A, D), 0.02),
        "a_ln_g": 1.0 + nrm(ks[6], (N_A, D), 0.02),
        "a_ln_b": nrm(ks[7], (N_A, D), 0.02),
        "a_w_pw2": nrm(ks[8], (N_A, D, D), BETA * D ** -0.5),
        "b_w_in": nrm(ks[9], (N_B, D, 2 * E), D ** -0.5),
        "b_b_in": nrm(ks[10], (N_B, 2 * E), 0.02),
        "b_ln_g": 1.0 + nrm(ks[11], (N_B, E), 0.02),
        "b_ln_b": nrm(ks[12], (N_B, E), 0.02),
        "b_w_s": nrm(ks[13], (N_B, SGU_HEADS, SGU_BLOCK, SGU_BLOCK), SGU_BLOCK ** -0.5),
        "b_b_s": 1.0 + nrm(ks[14], (N_B, SGU_HEADS, SGU_BLOCK), 0.02),
        "b_w_out": nrm(ks[15], (N_B, E, D), BETA * E ** -0.5),
        "c_w_in": nrm(ks[16], (N_C, D, 3 * D), D ** -0.5),
        "c_w_conv": nrm(ks[17], (N_C, CONV_C_WIDTH, D), CONV_C_WIDTH ** -0.5),
        "c_w_out": nrm(ks[18], (N_C, D, D), BETA * D ** -0.5),
        "ln1_g": 1.0 + nrm(ks[19], (DEPTH, D), 0.02),
        "ln1_b": nrm(ks[20], (DEPTH, D), 0.02),
        "ln2_g": 1.0 + nrm(ks[21], (DEPTH, D), 0.02),
        "ln2_b": nrm(ks[22], (DEPTH, D), 0.02),
        "ffn_w_gate": nrm(ks[23], (DEPTH, D, D_FF), D ** -0.5),
        "ffn_w_up": nrm(ks[24], (DEPTH, D, D_FF), D ** -0.5),
        "ffn_w_down": nrm(ks[25], (DEPTH, D_FF, D), BETA * D_FF ** -0.5),
        "ple_w_gate": nrm(ks[26], (DEPTH, D, D), D ** -0.5),
        "ple_w_proj": nrm(ks[27], (DEPTH, D_PLE, D), D_PLE ** -0.5),
        "ple_norm_g": 1.0 + nrm(ks[28], (DEPTH, D), 0.02),
    }

def reference(x, p,
              a_w_pw1, a_b_pw1, a_w_dw, a_b_dw, a_ln_g, a_ln_b, a_w_pw2,
              b_w_in, b_b_in, b_ln_g, b_ln_b, b_w_s, b_b_s, b_w_out,
              c_w_in, c_w_conv, c_w_out,
              ln1_g, ln1_b, ln2_g, ln2_b,
              ffn_w_gate, ffn_w_up, ffn_w_down,
              ple_w_gate, ple_w_proj, ple_norm_g):
    for i in range(DEPTH):
        m, j = i % N_MIXERS, i // N_MIXERS
        if m == 0:
            h = mixer_conformer_conv(x, a_w_pw1[j], a_b_pw1[j], a_w_dw[j], a_b_dw[j],
                                     a_ln_g[j], a_ln_b[j], a_w_pw2[j])
        elif m == 1:
            h = mixer_sgu(x, b_w_in[j], b_b_in[j], b_ln_g[j], b_ln_b[j],
                          b_w_s[j], b_b_s[j], b_w_out[j])
        else:
            h = mixer_short_conv(x, c_w_in[j], c_w_conv[j], c_w_out[j])
        x = layer_norm(ALPHA * x + h, ln1_g[i], ln1_b[i])
        x = layer_norm(ALPHA * x + swiglu(x, ffn_w_gate[i], ffn_w_up[i], ffn_w_down[i]),
                       ln2_g[i], ln2_b[i])
        gate = jax.nn.sigmoid(x @ ple_w_gate[i])
        x = x + gate * rms_norm(p[i] @ ple_w_proj[i], ple_norm_g[i])
    return x


_drawn_inputs = setup_inputs


def setup_inputs(seed=0):
    import zlib

    import numpy as np

    out = dict(_drawn_inputs(seed))
    spreads = {}
    factors = {'a_b_pw1': 8.0,
     'a_b_dw': 8.0,
     'a_ln_g': 54.896,
     'a_ln_b': 55.532,
     'b_b_in': 8.0,
     'b_ln_g': 64.0,
     'b_ln_b': 64.0,
     'b_b_s': 64.0,
     'ple_norm_g': 3.228,
     'ln1_g': 3.374,
     'ln1_b': 3.429,
     'ln2_g': 3.327,
     'ln2_b': 3.459}
    for name, (base, spread) in spreads.items():
        noise = np.random.default_rng([zlib.crc32(name.encode()), seed]).standard_normal(out[name].shape)
        drawn = base * np.exp(spread * noise) if base else spread * noise
        out[name] = __import__('jax').numpy.asarray(drawn.astype(out[name].dtype))
    for name, factor in factors.items():
        out[name] = (out[name] * factor).astype(out[name].dtype)
    return out
```

```python
from contextlib import ExitStack

import concourse.bass as bass
from concourse import mybir

ALU = mybir.AluOpType
ACT = mybir.ActivationFunctionType
F32 = mybir.dt.float32
F32R = mybir.dt.float32r

P = 128
BANK = 512
D_MODEL = 1024
SEQ = 512
DEPTH = 4
CHUNK = 64
TAPS_A = 31
TAPS_C = 3
TAPS_PE = 20
SGU_BLOCK = 128
SGU_HEADS = 8
SGU_WIDTH = 2 * D_MODEL
D_FF = 2816
D_PLE = 256
ALPHA = (2 * DEPTH) ** 0.25
EPS = 1e-5

DT = D_MODEL // P
FT = D_FF // P
ET = SGU_WIDTH // P
TT = SEQ // P
PAD = TAPS_A - 1
UK = 2
RING = 4
TILES = 4
LEAD = RING


class Group:

    def __init__(self, stage, index, g, unit, units, mark):
        self.stage, self.index, self.g, self.unit, self.units, self.mark = stage, index, g, unit, units, mark

    def used(self, ku):
        return self.mark + ku + 1 if ku < self.units - 1 else self.end()

    def tile(self, j):
        return self.mark + self.units - 1 + j + 1

    def end(self):
        return self.mark + self.units - 1 + TILES


class Stage:

    def __init__(self, kind, layer, k_tiles):
        self.kind, self.layer, self.k_tiles = kind, layer, k_tiles
        self.groups = []
        self.src0 = self.gate0 = self.prod0 = self.norm = self.out0 = self.stats_g = None


def plan():
    stages, freed = [], {}
    at = {"unit": 0, "g": 0, "mark": 0, "norm": 0, "x": DT, "gate": 0, "prod": 0}

    def stage(kind, layer, k_tiles, n_groups, source=DT, skip=None):
        s = Stage(kind, layer, k_tiles)
        s.src0 = at["x"] - source
        s.gate0, s.prod0 = at["gate"], at["prod"]
        gated = kind in ("conv_in", "short_in", "ffn_in")
        for i in range(n_groups):
            at["g"] += i == skip
            grp = Group(s, i, at["g"], at["unit"], k_tiles // UK, at["mark"])
            s.groups.append(grp)
            at["g"] += 1
            at["unit"] += grp.units
            at["mark"] = grp.end()
            if gated or kind == "ple_gate":
                at["gate"] += 1 if gated else 2
            if gated or kind == "short_gate":
                at["prod"] += 1
            freed[grp.g] = {
                "conv_in": ("prod_ready", at["prod"]), "short_in": ("prod_ready", at["prod"]),
                "ffn_in": ("prod_ready", at["prod"]), "short_gate": ("prod_ready", at["prod"]),
                "ple_gate": ("gate_ready", at["gate"]), "ple_proj": ("proj_freed", 2 * layer + i + 1),
                "sgu_u": ("gelu_u", i + 1), "sgu_v": ("vsum_ready", i + 1),
                "mixer_out": (("ysum_ready", at["norm"] + 1), ("z_ready", 5 * at["norm"] + 5))[i % 2],
                "ffn_out": (("ysum_ready", at["norm"] + 1), ("z_ready", 5 * at["norm"] + 5))[i % 2],
            }[kind]
        stages.append(s)
        return s

    def norm(s):
        s.norm, s.stats_g = at["norm"], at["g"]
        at["norm"] += 1
        freed[at["g"]] = ("var_ready", at["norm"])
        at["g"] += 1
        write(s)

    def write(s, tiles=DT):
        s.out0 = at["x"]
        at["x"] += tiles

    for layer in range(DEPTH):
        width = DT
        if layer % 3 == 0:
            s = stage("conv_in", layer, DT, 4)
            s.taps_g = at["g"]
            freed[at["g"]] = ("z_ready", 5 * at["norm"] + 5)
            at["g"] += 1
            norm(s)
        elif layer % 3 == 1:
            s = stage("sgu_v", layer, DT, 4, skip=1)
            s.table_g = s.groups[0].g + 1
            freed[s.table_g] = ("rowsum_saved", 1)
            s = stage("sgu_u", layer, DT, 4)
            s.mix_g = at["g"]
            for q in range(ET // TILES):
                freed[at["g"] + q] = ("uf_ready", TILES * (q + 1))
            at["g"] += ET // TILES
            width = ET
            write(s, ET)
        else:
            stage("short_in", layer, DT, 4)
            write(stage("short_gate", layer, DT, 2))
        norm(stage("mixer_out", layer, width, 2, source=width))
        stage("ffn_in", layer, DT, FT // 2)
        norm(stage("ffn_out", layer, FT, 2))
        stage("ple_proj", layer, D_PLE // P, 2)
        write(stage("ple_gate", layer, DT, 2))
    return stages, at, freed


ROWS = [("ln1_g", DEPTH), ("ln1_b", DEPTH), ("ln2_g", DEPTH), ("ln2_b", DEPTH), ("ple_norm_g", DEPTH),
        ("a_b_pw1", 4), ("a_b_dw", 2), ("a_ln_g", 2), ("a_ln_b", 2),
        ("b_b_in", 4), ("b_ln_g", 2), ("b_ln_b", 2), ("a_w_dw", 2 * TAPS_A), ("c_w_conv", TAPS_C)]
ROW0 = {}
N_ROWS = 0
for _name, _n in ROWS:
    ROW0[_name] = N_ROWS
    N_ROWS += _n * DT
ROW_TILES = -(-N_ROWS // P)
N_ROW_DMAS = sum((ROW0[_name] + _n * DT - 1) // P - ROW0[_name] // P + 1 for _name, _n in ROWS)


def trunk(nc, ins, out):
    stages, totals, freed = plan()
    by_kind = {}
    for s in stages:
        by_kind[s.kind, s.layer] = s

    ctx = ExitStack()
    with ctx:
        base = [nc.sbuf_base]

        def sb(name, words, dt=F32):
            at = -(-base[0] // 32) * 32
            base[0] = at + 4 * words
            return nc.alloc_sbuf_tensor_at(name, [P, words], dt, offset=at), at

        def also(name, words, dt, at):
            return nc.alloc_sbuf_tensor_at(name, [P, words], dt, offset=at)

        raw, _ = sb("raw", RING * UK * BANK)
        w_hi, _ = sb("w_hi", RING * UK * BANK, F32R)
        w_lo, _ = sb("w_lo", RING * UK * BANK, F32R)
        xf, _ = sb("xf", DT * SEQ)
        a_hi, a_at = sb("a_hi", DT * SEQ, F32R)
        a_lo, _ = sb("a_lo", DT * SEQ, F32R)
        a_f32 = also("a_f32", 2 * DT * SEQ, F32, a_at)
        h_hi, h_at = sb("h_hi", FT * SEQ, F32R)
        h_lo, _ = sb("h_lo", FT * SEQ, F32R)
        h_f32 = also("h_f32", 2 * FT * SEQ, F32, h_at)
        tmp, _ = sb("tmp", 6 * SEQ)
        mean, _ = sb("mean", SEQ)
        var, _ = sb("var", SEQ)
        rstd, rstd_at = sb("rstd", SEQ)
        ysum = also("ysum", SEQ, F32R, rstd_at)
        prm, _ = sb("prm", ROW_TILES * P)
        ident, _ = sb("ident", P)
        ones, _ = sb("ones", P)
        ones_r, _ = sb("ones_r", P, F32R)
        small, _ = sb("small", 128)
        assert base[0] <= nc.sbuf_usable_end, (base[0], nc.sbuf_usable_end)

        psum = ctx.enter_context(nc.psum_tensor("psum", [P, 8 * BANK], F32))

        raw_u = [raw[:, r * UK * BANK:(r + 1) * UK * BANK] for r in range(RING)]
        hi_u = [w_hi[:, r * UK * BANK:(r + 1) * UK * BANK] for r in range(RING)]
        lo_u = [w_lo[:, r * UK * BANK:(r + 1) * UK * BANK] for r in range(RING)]

        def tiles(t, m, n=1, width=SEQ):
            return t[:, m * width:(m + n) * width]

        def tile3(t, m, n, width=SEQ):
            return tiles(t, m, n, width).rearrange("p (n s) -> p n s", n=n)

        def many(ap, n):
            return ap.rearrange("p (o w) -> p o w", o=1).broadcast_to([P, n, ap.shape[1]])

        def bank(g, j, n=1):
            b = (g % 2) * TILES + j
            return psum[:, b * BANK:(b + n) * BANK]

        def banks3(g, j, n):
            return bank(g, j, n).rearrange("p (n s) -> p n s", n=n)

        def col(name, vec, m=0):
            c = ROW0[name] + vec * DT + m
            return prm[:, c:c + 1]

        HL = FT
        CONV_AT = 8 * SEQ
        CW = PAD + SEQ
        conv_x = h_f32[:, CONV_AT:CONV_AT + DT * CW].rearrange("p (m s) -> p m s", m=DT)
        CONV_Y = HL + 8
        PROJ = 8
        PROJ_SQ = HL + 8
        V_BIAS, ROW_SUM, B_S, W_T, W_S = HL + 10, HL + 14, HL + 16, HL + 18, HL + 20

        def u_tile(f):
            return (8 + f, h_hi, 8 + f) if f < FT - 8 else (HL + 8 + f - (FT - 8), h_lo, 8 + f - (FT - 8))

        p_raw = tile3(a_f32, 4, 2).rearrange("p n s -> p (n s)")
        pt_hi, pt_lo = tiles(a_hi, 6, 2), tiles(a_lo, 6, 2)
        x_in = a_f32[:, 0:TT * D_MODEL]
        v = a_f32[:, 0:TT * SGU_WIDTH].rearrange("p (t e) -> p t e", t=TT)

        DIAG_A = 2 * DT * SEQ // (TILES * P)
        DIAG_H = CONV_AT // SEQ + -(-DT * CW // SEQ)
        assert TAPS_PE - DIAG_A <= SEQ // P and DIAG_H + TILES <= HL

        def diag(i, k):
            at = (i * DIAG_A + k) * P
            return a_f32[:, at:at + P] if k < DIAG_A else tiles(h_f32, DIAG_H + i)[:, (k - DIAG_A) * P:(k - DIAG_A + 1) * P]

        def following(s):
            return stages[stages.index(s) + 1]

        def ffn_in(layer):
            return next(s for s in stages if s.kind == "ffn_in" and s.layer == layer)

        def sem(name):
            return ctx.enter_context(nc.semaphore(name))

        raw_landed = [sem(f"raw_landed{r}") for r in range(RING)]
        hi_ready = sem("hi_ready")
        lo_ready = sem("lo_ready")
        pe_done = sem("pe_done")
        x_hi_ready = sem("x_hi_ready")
        x_ready = sem("x_ready")
        gate_ready = sem("gate_ready")
        prod_ready = sem("prod_ready")
        prod_hi = sem("prod_hi")
        hidden_ready = sem("hidden_ready")
        ysum_ready = sem("ysum_ready")
        centre_done = sem("centre_done")
        centre_saved = sem("centre_saved")
        z_ready = sem("z_ready")
        sq_ready = sem("sq_ready")
        part_summed = sem("part_summed")
        sums_ready = sem("sums_ready")
        stats_done = sem("stats_done")
        mean_saved = sem("mean_saved")
        var_ready = sem("var_ready")
        std_ready = sem("std_ready")
        norm_ready = sem("norm_ready")
        affine_ready = sem("affine_ready")
        diag_ready = sem("diag_ready")
        taps_done = sem("taps_done")
        proj_sq = sem("proj_sq")
        proj_freed = sem("proj_freed")
        rms_sums = sem("rms_sums")
        rms_done = sem("rms_done")
        rms_var = sem("rms_var")
        rms_std = sem("rms_std")
        upd_ready = sem("upd_ready")
        pt_done = sem("pt_done")
        pt_hi_ready = sem("pt_hi_ready")
        pt_ready = sem("pt_ready")
        p_landed = sem("p_landed")
        gelu_u = sem("gelu_u")
        vsum_ready = sem("vsum_ready")
        gelu_v = sem("gelu_v")
        vvar_ready = sem("vvar_ready")
        vstd_ready = sem("vstd_ready")
        v_ready = sem("v_ready")
        ws_t_done = sem("ws_t_done")
        ws_t_ready = sem("ws_t_ready")
        rowsum_done = sem("rowsum_done")
        rowsum_saved = sem("rowsum_saved")
        mix_done = sem("mix_done")
        uf_ready = sem("uf_ready")
        sgu_landed = sem("sgu_landed")
        x_landed = sem("x_landed")
        row_landed = sem("row_landed")
        const_ready = sem("const_ready")
        prm_t_done = sem("prm_t_done")
        prm_ready = sem("prm_ready")
        x_t_done = sem("x_t_done")
        xf_ready = sem("xf_ready")
        out_t_done = sem("out_t_done")
        out_copied = sem("out_copied")
        out_landed = sem("out_landed")
        dve_step = sem("dve_step")
        act_step = sem("act_step")
        by_name = {"prod_ready": prod_ready, "gate_ready": gate_ready, "proj_freed": proj_freed, "gelu_u": gelu_u,
                   "vsum_ready": vsum_ready, "ysum_ready": ysum_ready, "z_ready": z_ready,
                   "var_ready": var_ready, "rowsum_saved": rowsum_saved, "uf_ready": uf_ready}

        block = ctx.enter_context(nc.Block())

        class Steps:

            def __init__(self, eng, s):
                self.eng, self.s, self.n = eng, s, 0

            def add(self, ins_):
                ins_.then_inc(self.s, 1)
                self.n += 1

            def settle(self, back=0):
                if self.n > back:
                    self.eng.wait_ge(self.s, self.n - back)

        def w_src(stage):
            L, k = stage.layer, stage.kind
            view = lambda ap: ap.rearrange("(a p) n -> p a n", p=P)
            if k == "conv_in":
                return view(ins["a_w_pw1"][L // 3]), ((0, 256), (D_MODEL, 256))
            if k == "sgu_u":
                return view(ins["b_w_in"][0]), ((0, 512),)
            if k == "sgu_v":
                return view(ins["b_w_in"][0]), ((SGU_WIDTH, 512),)
            if k == "short_in":
                return view(ins["c_w_in"][0]), ((D_MODEL, 256), (2 * D_MODEL, 256))
            if k == "short_gate":
                return view(ins["c_w_in"][0]), ((0, 512),)
            if k == "mixer_out":
                w = (ins["a_w_pw2"][L // 3], ins["b_w_out"][0], ins["c_w_out"][0])[L % 3]
                return view(w), ((0, 512),)
            if k == "ffn_out":
                return view(ins["ffn_w_down"][L]), ((0, 512),)
            if k == "ple_proj":
                return view(ins["ple_w_proj"][L]), ((0, 512),)
            if k == "ple_gate":
                return view(ins["ple_w_gate"][L]), ((0, 512),)
            assert False, k

        @block.sync
        def _(sp):
            sp.dma_start(x_in.rearrange("p (t d) -> p t d", t=TT),
                         ins["x"][0].rearrange("(t p) d -> p t d", p=P)).then_inc(x_landed, 16)
            n_dma = 0
            for name, n in ROWS:
                ap = ins[name]
                ap = ap.rearrange("a b n -> (a b n)") if len(ap.shape) == 3 else ap.rearrange("a n -> (a n)")
                rows = ap.rearrange("(r c) -> r c", c=P)
                r, end = ROW0[name], ROW0[name] + n * DT
                while r < end:
                    k = min(end, (r // P + 1) * P) - r
                    sp.dma_start(h_f32[r % P:r % P + k, CONV_Y * SEQ + (r // P) * P:CONV_Y * SEQ + (r // P + 1) * P],
                                 rows[r - ROW0[name]:r - ROW0[name] + k, :]).then_inc(row_landed, 16)
                    n_dma += 1
                    r += k
            assert n_dma == N_ROW_DMAS

            def load(slot, count, wait, view, k0, halves):
                if wait is not None:
                    sp.wait_ge(lo_ready, wait)
                dst = raw_u[slot].rearrange("p (a n) -> p a n", a=UK)
                if len(halves) == 2:
                    for i, c in enumerate(halves):
                        sp.dma_start(dst[:, :, i * 256:(i + 1) * 256],
                                     view[:, k0:k0 + UK, bass.ds(c, 256)]).then_inc(raw_landed[slot], 16)
                else:
                    for i in range(UK):
                        sp.dma_start(dst[:, i, :], view[:, k0 + i, halves[0]:halves[0] + BANK])\
                          .then_inc(raw_landed[slot], 16)

            for s in stages:
                if s.kind == "ffn_in":
                    for gate, up in ((ins["ffn_w_gate"][s.layer], ins["ffn_w_up"][s.layer]),):
                        gv = gate.rearrange("(a p) n -> p a n", p=P)
                        uv = up.rearrange("(a p) n -> p a n", p=P)

                        def ffn_unit(slot, wait, k0, c):
                            sp.wait_ge(lo_ready, wait)
                            dst = raw_u[slot].rearrange("p (a n) -> p a n", a=UK)
                            sp.dma_start(dst[:, :, 0:256], gv[:, k0:k0 + UK, bass.ds(c, 256)])\
                              .then_inc(raw_landed[slot], 16)
                            sp.dma_start(dst[:, :, 256:512], uv[:, k0:k0 + UK, bass.ds(c, 256)])\
                              .then_inc(raw_landed[slot], 16)

                        g0 = s.groups[0]
                        for ku in range(g0.units):
                            ffn_unit(ku % RING, g0.unit + ku - RING + 1, ku * UK, 0)
                        with sp.Fori(0, (len(s.groups) - 1) // 2) as it:
                            for i in range(2):
                                for ku in range(g0.units):
                                    u = g0.unit + g0.units * (1 + i) + ku
                                    ffn_unit(u % RING, it * (2 * g0.units) + (u - RING + 1), ku * UK,
                                             it * 512 + 256 * (1 + i))
                    continue
                view, parts = w_src(s)
                for grp in s.groups:
                    for ku in range(grp.units):
                        u = grp.unit + ku
                        if s.kind == "ffn_out" and grp.index == 0 and ku == 9:
                            sp.wait_ge(pe_done, s.groups[0].mark)
                            sp.dma_start(p_raw.rearrange("p (t d) -> p t d", t=TT),
                                         ins["p"][s.layer, 0].rearrange("(t p) d -> p t d", p=P))\
                              .then_inc(p_landed, 16)
                        load(u % RING, u // RING, u - RING + 1 if u >= RING else None,
                             view, ku * UK, [c + st * grp.index for c, st in parts])
                        if s.kind == "sgu_v" and grp.index == 1 and ku == 3:
                            sp.wait_ge(pe_done, s.groups[0].mark)
                            sp.dma_start(tiles(h_f32, V_BIAS, 4), ins["b_b_in"][0:1, SGU_WIDTH:2 * SGU_WIDTH]
                                         .broadcast_to([P, SGU_WIDTH])).then_inc(sgu_landed, 16)
                            sp.dma_start(tiles(h_f32, B_S, 2), ins["b_b_s"].rearrange("a h t -> a (h t)")
                                         .broadcast_to([P, SGU_HEADS * SGU_BLOCK])).then_inc(sgu_landed, 16)
                            sp.dma_start(tiles(h_f32, W_S, 2).rearrange("p (h s) -> p h s", h=SGU_HEADS),
                                         ins["b_w_s"][0].rearrange("h t s -> t h s")).then_inc(sgu_landed, 16)
            for half in range(2):
                sp.wait_ge(out_copied, half + 1)
                sp.dma_start(out[0].rearrange("(t p) d -> p t d", p=P)[:, :, half * BANK:(half + 1) * BANK],
                             tile3(a_f32, TT * half, TT)).then_inc(out_landed, 16)
            sp.wait_ge(out_landed, 32)

        @block.gpsimd
        def _(pool):
            pool.memset(ident[:, :], 0.0).then_inc(const_ready, 1)
            pool.memset(ones[:, :], 1.0 / D_MODEL).then_inc(const_ready, 1)
            pool.wait_ge(const_ready, 1)
            pool.affine_select(out=ident[:, :], in_=ident[:, :], compare_op=ALU.not_equal, fill=1.0,
                               base=0, pattern=[[-1, P]], channel_multiplier=1).then_inc(const_ready, 1)
            assert totals["unit"] % RING == 0
            with pool.Fori(0, totals["unit"] // RING) as it:
                for r in range(RING):
                    pool.wait_ge(hi_ready, it * RING + (r + 1))
                    pool.tensor_tensor(lo_u[r], raw_u[r], hi_u[r].bitcast(F32), ALU.subtract)\
                        .then_inc(lo_ready, 1)

        @block.tensor
        def _(pe):
            pe.wait_ge(const_ready, 3)
            pe.wait_ge(x_landed, 16)
            for m in range(DT):
                if m >= TILES:
                    pe.wait_ge(xf_ready, m - TILES + 1)
                for t in range(TT):
                    last = pe.transpose(psum[:, (m % TILES) * BANK + t * P:(m % TILES) * BANK + (t + 1) * P],
                                        x_in[:, t * D_MODEL + m * P:t * D_MODEL + (m + 1) * P], ident[:, :])
                last.then_inc(x_t_done, 1)
            pe.wait_ge(row_landed, 16 * N_ROW_DMAS)
            for r in range(ROW_TILES):
                k = min(P, N_ROWS - r * P)
                pe.transpose(psum[:, TILES * BANK + r * P:TILES * BANK + r * P + k],
                             h_f32[0:k, CONV_Y * SEQ + r * P:CONV_Y * SEQ + (r + 1) * P],
                             ident[0:k, 0:k]).then_inc(prm_t_done, 1)
            pe.wait_ge(xf_ready, DT)

            def take_half(g):
                if g >= 2:
                    name, count = freed[g - 2]
                    pe.wait_ge(by_name[name], count)
                elif g == 1:
                    pe.wait_ge(prm_ready, 2)

            def operands(slot, a, j, hi, lo, by_token):
                if by_token:
                    return (*(x[:, j * P:(j + 1) * P] for x in (hi, lo)),
                            *(x[slot][:, a * BANK:(a + 1) * BANK] for x in (hi_u, lo_u)))
                return (*(x[slot][:, a * BANK + j * P:a * BANK + (j + 1) * P] for x in (hi_u, lo_u)), hi, lo)

            def unit_by_k(s, grp, ku, waits):
                slot, by_token = (grp.unit + ku) % RING, s.kind == "sgu_v"
                for a in range(UK):
                    k = ku * UK + a
                    hi, lo = source(s, k)
                    if waits:
                        pe.wait_ge(x_hi_ready, s.src0 + k + 1)
                        for j in range(TILES):
                            st_hi, st_lo, mv_hi, mv_lo = operands(slot, a, j, hi, lo, by_token)
                            st, mv = (st_hi, mv_lo) if by_token else (st_lo, mv_hi)
                            pe.matmul(bank(grp.g, j), st, mv, start=(k == 0), stop=False)
                            pe.matmul(bank(grp.g, j), st_hi, mv_hi, start=False, stop=False)
                        pe.wait_ge(x_ready, s.src0 + k + 1)
                        for j in range(TILES):
                            st_hi, st_lo, mv_hi, mv_lo = operands(slot, a, j, hi, lo, by_token)
                            st, mv = (st_lo, mv_hi) if by_token else (st_hi, mv_lo)
                            done = pe.matmul(bank(grp.g, j), st, mv, start=False, stop=False)
                        continue
                    for j in range(TILES):
                        st_hi, st_lo, mv_hi, mv_lo = operands(slot, a, j, hi, lo, by_token)
                        pe.matmul(bank(grp.g, j), st_lo, mv_hi, start=(k == 0), stop=False)
                        pe.matmul(bank(grp.g, j), st_hi, mv_lo, start=False, stop=False)
                        done = pe.matmul(bank(grp.g, j), st_hi, mv_hi, start=False, stop=False)
                done.then_inc(pe_done, 1)

            def unit_by_tile(s, grp, ku, waits):
                slot, by_token = (grp.unit + ku) % RING, s.kind == "sgu_v"
                if waits:
                    pe.wait_ge(x_ready, s.src0 + (ku + 1) * UK)
                for j in range(TILES):
                    for a in range(UK):
                        k = ku * UK + a
                        st_hi, st_lo, mv_hi, mv_lo = operands(slot, a, j, *source(s, k), by_token)
                        pe.matmul(bank(grp.g, j), st_lo, mv_hi, start=(k == 0), stop=False)
                        pe.matmul(bank(grp.g, j), st_hi, mv_lo, start=False, stop=False)
                        done = pe.matmul(bank(grp.g, j), st_hi, mv_hi, start=False, stop=(a == UK - 1))
                    done.then_inc(pe_done, 1)

            def source(s, k):
                if s.kind in ("conv_in", "sgu_u", "sgu_v", "short_in", "short_gate", "ffn_out"):
                    return tiles(h_hi, k), tiles(h_lo, k)
                if s.kind == "mixer_out" and s.layer % 3 == 1:
                    hi = tiles(h_hi, k) if k < DT else tiles(h_lo, k - DT)
                    _, t, m = u_tile(k)
                    return hi, tiles(t, m)
                if s.kind == "ple_proj":
                    return tiles(pt_hi, k), tiles(pt_lo, k)
                return tiles(a_hi, k), tiles(a_lo, k)

            def centre(s):
                pe.wait_ge(ysum_ready, s.norm + 1)
                take_half(s.stats_g)
                pe.matmul(bank(s.stats_g, 0), ones_r[:, :], ysum[:, :], start=True, stop=True).then_inc(centre_done, 1)

            def stats(s):
                n = s.norm
                sum_z, sum_sq = bank(s.stats_g, 1), bank(s.stats_g, 2)
                z7 = tiles(h_f32, CONV_Y + DT - 1) if s.kind == "conv_in" else tiles(xf, DT - 1)
                pe.wait_ge(sums_ready, 2 * n + 1)
                pe.matmul(sum_z, ones[:, :], tiles(tmp, 5), start=True, stop=False)
                pe.wait_ge(z_ready, 5 * n + 5)
                pe.matmul(sum_z, ones[:, :], z7, start=False, stop=True).then_inc(stats_done, 1)
                pe.wait_ge(sq_ready, 5 * n + 5)
                pe.matmul(sum_sq, ones[:, :], tiles(tmp, 3), start=True, stop=False)
                pe.wait_ge(sums_ready, 2 * n + 2)
                pe.matmul(sum_sq, ones[:, :], tiles(tmp, 4), start=False, stop=True).then_inc(stats_done, 1)

            def embed(s, k):
                if k == 0:
                    pe.wait_ge(p_landed, 16 * (s.layer + 1))
                else:
                    pe.wait_ge(pt_ready, 2 * s.layer + k)
                o = bank(s.stats_g, 3)
                for t in range(TT):
                    last = pe.transpose(o[:, t * P:(t + 1) * P], p_raw[:, t * D_PLE + k * P:t * D_PLE + (k + 1) * P],
                                        ident[:, :])
                last.then_inc(pt_done, 1)

            def group(s, grp, u0):
                for ku in range(grp.units):
                    pe.wait_ge(lo_ready, u0 + (ku + 1))
                    if s.kind == "ffn_out" and grp.index == 0:
                        pe.wait_ge(hidden_ready, len(ffn_in(s.layer).groups) * s.layer + ku + 1)
                    if s.kind == "ple_proj" and grp.index == 0:
                        pe.wait_ge(pt_ready, 2 * (s.layer + 1))
                    waits = grp.index == 0 and s.kind not in ("ffn_out", "ple_proj")
                    (unit_by_tile if ku == grp.units - 1 else unit_by_k)(s, grp, ku, waits)
                    if grp.index == 1 and s.kind in ("mixer_out", "ffn_out"):
                        if ku == 1:
                            centre(s)
                        if ku == 2 and s.kind == "ffn_out":
                            embed(s, 0)
                        if ku == 5 and s.kind == "ffn_out":
                            embed(s, 1)
                    if s.kind == "ple_gate" and grp.index == 0 and ku == 2:
                        pe.wait_ge(rms_sums, s.layer + 1)
                        take_half(grp.g + 1)
                        pe.matmul(bank(grp.g + 1, 0), ones[:, :], tiles(h_f32, PROJ_SQ), start=True, stop=True)\
                            .then_inc(rms_done, 1)

            for s in stages:
                for grp in s.groups[:1] if s.kind == "ffn_in" else s.groups:
                    if s.kind == "ple_gate" and grp.index == 1:
                        pe.wait_ge(rms_var, s.layer + 1)
                    take_half(grp.g)
                    group(s, grp, grp.unit)
                    if s.kind == "sgu_v" and grp.index == 0:
                        take_half(s.table_g)
                        pe.wait_ge(sgu_landed, 48)
                        for h in range(SGU_HEADS):
                            last = pe.transpose(bank(s.table_g, 0, 2)[:, h * P:(h + 1) * P],
                                                tiles(h_f32, W_S, 2)[:, h * P:(h + 1) * P], ident[:, :])
                        last.then_inc(ws_t_done, 1)
                    if s.kind == "sgu_v" and grp.index == 1:
                        pe.wait_ge(ws_t_ready, 1)
                        for i in range(2):
                            last = pe.matmul(bank(s.table_g, 2 + i), ones[:, :], tiles(h_f32, W_T + i),
                                             start=True, stop=True)
                        last.then_inc(rowsum_done, 1)
                    if s.kind == "ple_proj" and grp.index == 0:
                        stats(stages[stages.index(s) - 1])
                if s.kind == "ffn_in":
                    per = 2 * s.groups[0].units
                    with pe.Fori(0, (len(s.groups) - 1) // 2) as it:
                        for grp in s.groups[1:3]:
                            pe.wait_ge(prod_ready, it * 2 + (s.prod0 + grp.index - 1))
                            group(s, grp, it * per + grp.unit)
                if s.kind == "conv_in":
                    take_half(s.taps_g)
                    for i in range(TILES):
                        pe.wait_ge(prod_ready, s.prod0 + 3 + i // 2)
                        pe.wait_ge(diag_ready, TILES * (s.layer // 3) + i + 1)
                        for k in range(TAPS_PE):
                            last = pe.matmul(bank(s.taps_g, i), diag(i, k), conv_x[:, TILES + i, k:k + SEQ],
                                             start=(k == 0), stop=(k == TAPS_PE - 1))
                        last.then_inc(taps_done, 1)
                        if i == 1:
                            centre(s)
                    stats(s)
                if s.kind == "mixer_out":
                    stats(s)
                if s.kind == "sgu_u":
                    pe.wait_ge(v_ready, TT)
                    for f in range(ET):
                        g = s.mix_g + f // TILES
                        if f % TILES == 0:
                            take_half(g)
                        head = f * P // (SGU_WIDTH // SGU_HEADS)
                        for t in range(TT):
                            last = pe.matmul(bank(g, f % TILES)[:, t * P:(t + 1) * P],
                                             v[:, t, f * P:(f + 1) * P],
                                             tiles(h_f32, W_T, 2)[:, head * P:(head + 1) * P], start=True, stop=True)
                        last.then_inc(mix_done, 1)
            for half in range(2):
                g = stages[-1].groups[half].g
                pe.wait_ge(gate_ready, totals["gate"] - 2 + 2 * half)
                for m in range(TILES * half, TILES * (half + 1)):
                    pe.wait_ge(upd_ready, DT * (DEPTH - 1) + m + 1)
                    for t in range(TT):
                        last = pe.transpose(bank(g, t)[:, (m % TILES) * P:(m % TILES + 1) * P],
                                            xf[:, m * SEQ + t * P:m * SEQ + (t + 1) * P], ident[:, :])
                last.then_inc(out_t_done, 1)

        @block.scalar
        def _(act):
            own = Steps(act, act_step)
            act.wait_ge(const_ready, 3)

            def split(r, landed, used):
                act.wait_ge(raw_landed[r], landed)
                if used is not None:
                    act.wait_ge(pe_done, used)
                act.copy(hi_u[r], raw_u[r]).then_inc(hi_ready, 1)

            used = []
            for s in stages:
                for grp in s.groups:
                    used += [grp.used(ku) for ku in range(grp.units)]

            split_end = [0]

            def split_to(end):
                for u in range(split_end[0], min(end, totals["unit"])):
                    split(u % RING, 32 * (u // RING + 1), used[u - RING] if u >= RING else None)
                split_end[0] = max(end, split_end[0])

            split_to(LEAD)
            for m in range(DT):
                act.wait_ge(xf_ready, m + 1)
                act.copy(tiles(h_hi, m), tiles(xf, m)).then_inc(x_hi_ready, 1)
            act.copy(ones_r[:, :], ones[:, :]).then_inc(prm_ready, 1)
            act.wait_ge(prm_t_done, ROW_TILES)
            act.copy(prm[:, 0:N_ROWS], psum[:, TILES * BANK:TILES * BANK + N_ROWS]).then_inc(prm_ready, 1)
            act.wait_ge(prm_ready, 2)

            def load_sqrt():
                own.settle()
                own.add(act.activation(small[:, 120:121], ones[:, 0:1], ACT.Sqrt))

            def norm_first(s, z):
                n = s.norm
                act.wait_ge(centre_done, n + 1)
                act.activation(mean[:, :], bank(s.stats_g, 0), ACT.Copy, scale=2.0).then_inc(centre_saved, 1)
                if s.kind == "ffn_out":
                    embed(s, 0)
                act.wait_ge(z_ready, 5 * n + 1)
                act.activation(tiles(tmp, 0, 4), z(0, 4), ACT.Square).then_inc(sq_ready, 1)

            def embed(s, k):
                act.wait_ge(pt_done, 2 * s.layer + k + 1)
                act.copy(tiles(pt_hi, k), bank(s.stats_g, 3)).then_inc(pt_hi_ready, 1)

            def norm_second(s, z):
                n = s.norm
                act.wait_ge(part_summed, n + 1)
                for j in range(TILES):
                    act.wait_ge(z_ready, 5 * n + 2 + j)
                    act.activation(tiles(tmp, j), z(TILES + j, 1), ACT.Square).then_inc(sq_ready, 1)

            def norm_root(s):
                n = s.norm
                load_sqrt()
                act.wait_ge(stats_done, 2 * n + 1)
                act.activation(var[:, :], bank(s.stats_g, 1), ACT.Square).then_inc(mean_saved, 1)
                act.copy(mean[:, :], bank(s.stats_g, 1)).then_inc(mean_saved, 1)
                act.wait_ge(var_ready, n + 1)
                act.activation(var[:, :], var[:, :], ACT.Sqrt).then_inc(std_ready, 1)

            def norm_finish(s, z, func, gain, bias, vec, out_hi):
                n = s.norm
                for m in range(DT):
                    act.wait_ge(norm_ready, DT * n + m + 1)
                    if s.kind == "ffn_out" and m == 6:
                        act.wait_ge(pe_done, following(s).groups[1].end())
                    affine = {"bias": col(bias, vec, m), "scale": col(gain, vec, m)}
                    act.activation(tiles(out_hi, m), z(m, 1), func, **affine).then_inc(x_hi_ready, 1)
                    act.wait_ge(x_hi_ready, s.out0 + m + 1)
                    act.activation(z(m, 1), z(m, 1), func, **affine).then_inc(affine_ready, 1)
                    if s.kind == "ffn_out" and m in (2, 4):
                        split_to(split_end[0] + 1)
                    if s.kind == "ffn_out" and m == 5:
                        proj_squares(following(s), 1)

            def hi_of(ready, count, out, tile):
                act.wait_ge(ready, count)
                act.copy(out, tile).then_inc(x_hi_ready, 1)

            def ffn_in_epilogue(grp, marks, prods, hidden):
                gate = tiles(tmp, 2 * (grp.g % 2), 2)
                act.wait_ge(pe_done, marks + grp.units + 1)
                act.activation(gate, bank(grp.g, 0, 2), ACT.Silu).then_inc(gate_ready, 1)
                act.wait_ge(prod_ready, prods)
                act.copy(h_hi[:, hidden], tiles(tmp, 4, 2)).then_inc(prod_hi, 1)

            def epilogue(s, grp):
                g = grp.g
                z = lambda m, n: tiles(xf, m, n)
                if s.kind == "conv_in":
                    for i in range(2):
                        act.wait_ge(pe_done, grp.tile(2 + i))
                        ins_ = act.activation(tiles(tmp, 2 * (g % 2) + i), bank(g, 2 + i), ACT.Sigmoid,
                                              bias=col("a_b_pw1", 2 * (s.layer // 3) + 1, 2 * grp.index + i))
                        own.add(ins_) if i == 0 else ins_.then_inc(gate_ready, 1)
                    for k in range(TAPS_PE):
                        ins_ = act.activation(diag(grp.index, k), ident[:, :], ACT.Copy,
                                              scale=col("a_w_dw", s.layer // 3 * TAPS_A + k, TILES + grp.index))
                        own.add(ins_) if k < TAPS_PE - 1 else ins_.then_inc(diag_ready, 1)
                    if grp.index == 3:
                        y = lambda m, n: tiles(h_f32, CONV_Y + m, n)
                        act.wait_ge(prod_ready, s.prod0 + 4)
                        norm_first(s, y)
                        norm_second(s, y)
                        norm_root(s)
                        norm_finish(s, y, ACT.Silu, "a_ln_g", "a_ln_b", s.layer // 3, a_hi)
                if s.kind == "short_in":
                    act.wait_ge(pe_done, grp.tile(1))
                    act.copy(tiles(tmp, 2 * (g % 2), 2), bank(g, 0, 2)).then_inc(gate_ready, 1)
                if s.kind == "short_gate":
                    act.wait_ge(prod_ready, s.prod0 + grp.index + 1)
                    for m in range(TILES * grp.index, TILES * (grp.index + 1)):
                        act.copy(tiles(a_hi, m), tiles(h_f32, CONV_Y + m)).then_inc(x_hi_ready, 1)
                if s.kind == "sgu_u":
                    for j in range(TILES):
                        f = TILES * grp.index + j
                        act.wait_ge(pe_done, grp.tile(j))
                        ins_ = act.activation(tiles(h_f32, u_tile(f)[0]), bank(g, j), ACT.Gelu_apprx_tanh,
                                              bias=col("b_b_in", f // DT, f % DT))
                        own.add(ins_) if j < TILES - 1 else ins_.then_inc(gelu_u, 1)
                    if grp.index == 3:
                        for f in range(ET):
                            out = tiles(h_hi, f) if f < DT else tiles(h_lo, f - DT)
                            hi_of(uf_ready, f + 1, out, tiles(tmp, 4 + f % 2))
                if s.kind == "sgu_v":
                    act.wait_ge(vsum_ready, grp.index + 1)
                    vq = v[:, :, grp.index * BANK:(grp.index + 1) * BANK]
                    act.activation(vq, vq, ACT.Gelu_apprx_tanh).then_inc(gelu_v, 1)
                    if grp.index == 3:
                        act.wait_ge(vvar_ready, 1)
                        act.activation(small[:, 104:108], small[:, 104:108], ACT.Sqrt).then_inc(vstd_ready, 1)
                if s.kind in ("mixer_out", "ffn_out"):
                    if grp.index == 0:
                        norm_first(s, z)
                        if s.kind == "ffn_out":
                            split_to(s.groups[1].unit + 8)
                            embed(s, 1)
                    else:
                        norm_second(s, z)
                        if s.kind == "ffn_out":
                            proj_squares(following(s), 0)
                        norm_root(s)
                        which = "ln1" if s.kind == "mixer_out" else "ln2"
                        norm_finish(s, z, ACT.Identity, which + "_g", which + "_b", s.layer, a_hi)
                if s.kind == "ple_gate":
                    if grp.index == 0:
                        load_sqrt()
                        act.wait_ge(rms_var, s.layer + 1)
                        act.activation(var[:, :], var[:, :], ACT.Sqrt).then_inc(rms_std, 1)
                    else:
                        act.wait_ge(upd_ready, DT * s.layer + TILES)
                    for h in range(2):
                        act.wait_ge(pe_done, grp.tile(2 * h + 1))
                        act.activation(tiles(tmp, 2 * h, 2), bank(g, 2 * h, 2), ACT.Sigmoid).then_inc(gate_ready, 1)
                    if s.layer < DEPTH - 1:
                        for m in range(TILES * grp.index, TILES * (grp.index + 1)):
                            hi_of(upd_ready, DT * s.layer + m + 1, tiles(h_hi, m), tiles(xf, m))

            def proj_squares(s, i):
                act.wait_ge(proj_freed, 2 * s.layer + i + 1)
                act.activation(tiles(h_f32, PROJ_SQ + TILES * i, 4), tiles(h_f32, PROJ + TILES * i, 4), ACT.Square)\
                    .then_inc(proj_sq, 1)

            for s in stages:
                if s.kind != "ffn_in":
                    for grp in s.groups:
                        split_to(grp.unit + grp.units + LEAD)
                        epilogue(s, grp)
                    continue
                first = s.groups[0]
                split_to(first.unit + first.units + LEAD)
                ffn_in_epilogue(first, first.mark, s.prod0 + 1, slice(0, 2 * SEQ))
                n = first.units
                with act.Fori(0, (len(s.groups) - 1) // 2) as it:
                    for grp in s.groups[1:3]:
                        marks = it * (2 * (n - 1 + TILES)) + grp.mark
                        for ku in range(n):
                            u = grp.unit + n + ku
                            split(u % RING, it * (2 * n // RING * 32) + 32 * (u // RING + 1),
                                  marks + (grp.used(ku) - grp.mark))
                        ffn_in_epilogue(grp, marks, it * 2 + (s.prod0 + grp.index + 1),
                                        bass.ds(it * (4 * SEQ) + grp.index * 2 * SEQ, 2 * SEQ))
                split_end[0] = s.groups[-1].unit + n + LEAD
            for half in range(2):
                act.wait_ge(out_t_done, half + 1)
                act.copy(tiles(a_f32, TT * half, TT), bank(stages[-1].groups[half].g, 0, TT)).then_inc(out_copied, 1)

        @block.vector
        def _(dve):
            own = Steps(dve, dve_step)
            for m in range(DT):
                dve.wait_ge(x_t_done, m + 1)
                dve.tensor_copy(tiles(xf, m), psum[:, (m % TILES) * BANK:(m % TILES + 1) * BANK]).then_inc(xf_ready, 1)
            dve.wait_ge(xf_ready, DT)

            def lo_of(ready, count, out_lo, x, out_hi):
                dve.wait_ge(ready, count)
                dve.tensor_tensor(out_lo, x, out_hi.bitcast(F32), ALU.subtract).then_inc(x_ready, 1)

            for m in range(DT):
                lo_of(x_hi_ready, m + 1, tiles(h_lo, m), tiles(xf, m), tiles(h_hi, m))
            dve.wait_ge(prm_ready, 2)

            def three(ap, n):
                return ap.rearrange("p (n s) -> p n s", n=n)

            def norm_centre_sum(z):
                own.settle()
                own.add(dve.tensor_tensor(tiles(tmp, 4, 2), z(0, 2), z(2, 2), ALU.add))
                own.settle()
                dve.tensor_tensor(ysum[:, :], tiles(tmp, 4), tiles(tmp, 5), ALU.add).then_inc(ysum_ready, 1)

            def norm_sums(s, z):
                n = s.norm
                dve.wait_ge(z_ready, 5 * n + 1)
                own.add(dve.tensor_tensor(tiles(tmp, 4, 2), z(0, 2), z(2, 2), ALU.add))
                own.settle()
                own.add(dve.tensor_tensor(tiles(tmp, 5), tiles(tmp, 4), tiles(tmp, 5), ALU.add))
                dve.wait_ge(sq_ready, 5 * n + 1)
                own.add(dve.tensor_tensor(tiles(tmp, 0, 2), tiles(tmp, 0, 2), tiles(tmp, 2, 2), ALU.add))
                own.settle()
                dve.tensor_tensor(tiles(tmp, 4), tiles(tmp, 0), tiles(tmp, 1), ALU.add).then_inc(part_summed, 1)

            def norm_last(s, z, g, complete):
                n = s.norm
                sum_z, sum_sq = tiles(tmp, 5), tiles(tmp, 4)
                dve.wait_ge(part_summed, n + 1)
                own.settle()

                def add(total, what, done=None):
                    own.settle()
                    ins_ = dve.tensor_tensor(total, total, what, ALU.add)
                    own.add(ins_) if done is None else ins_.then_inc(done, 1)

                for j in range(TILES):
                    dve.wait_ge(*complete(j))
                    dve.tensor_tensor(z(TILES + j, 1), bank(g, j), z(TILES + j, 1), ALU.add).then_inc(z_ready, 1)
                    if j >= 1:
                        dve.wait_ge(z_ready, 5 * n + 1 + j)
                        add(sum_z, z(TILES + j - 1, 1), sums_ready if j == 3 else None)
                    if j >= 2:
                        dve.wait_ge(sq_ready, 5 * n + j)
                        add(sum_sq, tiles(tmp, j - 2))
                dve.wait_ge(sq_ready, 5 * n + 4)
                add(sum_sq, tiles(tmp, 2), sums_ready)

            def norm_root(s, z):
                n = s.norm
                dve.wait_ge(mean_saved, 2 * n + 2)
                own.add(dve.tensor_tensor(z(0, 1), z(0, 1), mean[:, :], ALU.subtract))
                dve.wait_ge(stats_done, 2 * n + 2)
                dve.scalar_tensor_tensor(var[:, :], bank(s.stats_g, 2), EPS, var[:, :], ALU.add, ALU.subtract)\
                   .then_inc(var_ready, 1)
                own.add(dve.tensor_tensor(z(1, 1), z(1, 1), mean[:, :], ALU.subtract))
                dve.wait_ge(std_ready, n + 1)
                own.add(dve.reciprocal(rstd[:, :], var[:, :]))

            def norm_finish(s, z, out_hi, out_lo):
                n = s.norm
                for m in range(DT + 1):
                    if m < DT:
                        if m >= 2:
                            own.add(dve.tensor_tensor(z(m, 1), z(m, 1), mean[:, :], ALU.subtract))
                        own.settle()
                        dve.tensor_tensor(z(m, 1), z(m, 1), rstd[:, :], ALU.mult).then_inc(norm_ready, 1)
                    if m >= 1:
                        lo_of(affine_ready, DT * n + m, tiles(out_lo, m - 1), z(m - 1, 1), tiles(out_hi, m - 1))
                    if s.kind == "ffn_out" and m == 4:
                        proj_out(following(s), 1)

            def residual_norm(s, grp):
                z = lambda m, n: tiles(xf, m, n)
                n = s.norm
                if grp.index == 0:
                    for h in range(2):
                        dve.wait_ge(pe_done, grp.tile(2 * h + 1))
                        own.add(dve.scalar_tensor_tensor(z(2 * h, 2), z(2 * h, 2), ALPHA, bank(grp.g, 2 * h, 2),
                                                         ALU.mult, ALU.add))
                    norm_centre_sum(z)
                    dve.wait_ge(centre_saved, s.norm + 1)
                    dve.tensor_tensor(three(z(0, 4), 4), three(z(0, 4), 4), many(mean[:, :], 4), ALU.subtract)\
                       .then_inc(z_ready, 1)
                    own.add(dve.scalar_tensor_tensor(three(z(4, 4), 4), three(z(4, 4), 4), ALPHA,
                                                     many(mean[:, :], 4), ALU.mult, ALU.subtract))
                    if s.kind == "ffn_out":
                        embed(s, 0)
                    norm_sums(s, z)
                    if s.kind == "ffn_out":
                        embed(s, 1)
                    own.settle()
                    return
                norm_last(s, z, grp.g, lambda j: (pe_done, grp.tile(j)))
                if s.kind == "ffn_out":
                    proj_out(following(s), 0)
                norm_root(s, z)
                norm_finish(s, z, a_hi, a_lo)

            def embed(s, k):
                dve.wait_ge(pt_hi_ready, 2 * s.layer + k + 1)
                dve.tensor_tensor(tiles(pt_lo, k), bank(s.stats_g, 3), tiles(pt_hi, k).bitcast(F32), ALU.subtract)\
                   .then_inc(pt_ready, 1)

            def proj_out(s, i):
                dve.wait_ge(pe_done, s.groups[i].end())
                dve.tensor_copy(tiles(h_f32, PROJ + TILES * i, 4), bank(s.groups[i].g, 0, 4)).then_inc(proj_freed, 1)

            def convolve(s, m0, w_name, w0, first, end, taps, bias, fresh=True):
                for k in range(first, end):
                    for m in (m0, m0 + 1):
                        x = conv_x[:, m, PAD - taps + 1 + k:PAD - taps + 1 + k + SEQ]
                        y = tiles(h_f32, CONV_Y + m)
                        w = col(w_name, w0 + k, m)
                        own.settle(back=1)
                        if k == first and fresh and bias is not None:
                            own.add(dve.tensor_scalar(y, x, w, col(bias, s.layer // 3, m), ALU.mult, ALU.add))
                        elif k == first and fresh:
                            own.add(dve.tensor_scalar(y, x, w, None, ALU.mult))
                        else:
                            own.add(dve.scalar_tensor_tensor(y, x, w, y, ALU.mult, ALU.add))

            def gated_input(s, grp):
                gate = tiles(tmp, 2 * (grp.g % 2), 2)
                dve.wait_ge(gate_ready, s.gate0 + grp.index + 1)
                for i in range(2):
                    m = 2 * grp.index + i
                    ins_ = dve.scalar_tensor_tensor(conv_x[:, m, PAD:PAD + SEQ], bank(grp.g, i),
                                                    col("a_b_pw1", 2 * (s.layer // 3), m), tiles(gate, i),
                                                    ALU.add, ALU.mult)
                    own.add(ins_) if i == 0 else ins_.then_inc(prod_ready, 1)
                dve.wait_ge(prod_ready, s.prod0 + grp.index + 1)

            def ffn_in_epilogue(grp, marks, gates, hidden, before=None):
                if before is not None:
                    dve.wait_ge(hidden_ready, before)
                gate = tiles(tmp, 2 * (grp.g % 2), 2)
                prod = tiles(tmp, 4, 2)
                dve.wait_ge(pe_done, marks + grp.units + 3)
                dve.wait_ge(gate_ready, gates[0])
                dve.tensor_tensor(prod, bank(grp.g, 2, 2), gate, ALU.mult).then_inc(prod_ready, 1)
                dve.wait_ge(prod_hi, gates[1])
                dve.tensor_tensor(h_lo[:, hidden], prod, h_hi[:, hidden].bitcast(F32), ALU.subtract)\
                   .then_inc(hidden_ready, 1)

            def epilogue(s, grp):
                g = grp.g
                if s.kind in ("conv_in", "short_in") and grp.index == 0:
                    dve.wait_ge(pe_done, grp.mark + 1)
                    own.add(dve.memset(conv_x[:, :, 0:PAD], 0.0))
                if s.kind == "short_in":
                    m0 = 2 * grp.index
                    dve.wait_ge(gate_ready, s.gate0 + grp.index + 1)
                    dve.wait_ge(pe_done, grp.end())
                    dve.tensor_tensor(conv_x[:, m0:m0 + 2, PAD:PAD + SEQ], banks3(g, 2, 2),
                                      three(tiles(tmp, 2 * (g % 2), 2), 2), ALU.mult).then_inc(prod_ready, 1)
                    dve.wait_ge(prod_ready, s.prod0 + grp.index + 1)
                    own.settle()
                    convolve(s, m0, "c_w_conv", 0, 0, TAPS_C, TAPS_C, None)
                if s.kind == "conv_in":
                    y = lambda m, n: tiles(h_f32, CONV_Y + m, n)
                    w = ("a_w_dw", s.layer // 3 * TAPS_A)
                    if grp.index == 0:
                        gated_input(s, s.groups[0])
                        own.settle()
                        convolve(s, 0, *w, 0, 18, TAPS_A, "a_b_dw")
                        gated_input(s, s.groups[1])
                        convolve(s, 0, *w, 18, TAPS_A, TAPS_A, "a_b_dw", fresh=False)
                        own.settle()
                        convolve(s, 2, *w, 0, 4, TAPS_A, "a_b_dw")
                    if grp.index == 2:
                        gated_input(s, s.groups[2])
                        convolve(s, 2, *w, 4, TAPS_A, TAPS_A, "a_b_dw", fresh=False)
                        norm_centre_sum(y)
                    if grp.index == 3:
                        gated_input(s, s.groups[3])
                        own.settle()
                        for m in (4, 6):
                            convolve(s, m, *w, TAPS_PE, TAPS_A, TAPS_A, "a_b_dw")
                        dve.wait_ge(centre_saved, s.norm + 1)
                        dve.tensor_tensor(three(y(0, 4), 4), three(y(0, 4), 4), many(mean[:, :], 4), ALU.subtract)\
                           .then_inc(z_ready, 1)
                        own.settle()
                        own.add(dve.tensor_tensor(three(y(4, 4), 4), three(y(4, 4), 4), many(mean[:, :], 4), ALU.subtract))
                        norm_sums(s, y)
                        norm_last(s, y, s.taps_g, lambda j: (taps_done, TILES * (s.layer // 3) + j + 1))
                        norm_root(s, y)
                        norm_finish(s, y, a_hi, a_lo)
                if s.kind == "short_gate":
                    own.settle()
                    y4 = tiles(h_f32, CONV_Y + TILES * grp.index, 4)
                    dve.wait_ge(pe_done, grp.end())
                    dve.tensor_tensor(y4, y4, bank(g, 0, 4), ALU.mult).then_inc(prod_ready, 1)
                    for m in range(TILES * grp.index, TILES * (grp.index + 1)):
                        lo_of(x_hi_ready, s.out0 + m + 1, tiles(a_lo, m), tiles(h_f32, CONV_Y + m), tiles(a_hi, m))
                if s.kind == "sgu_v":
                    q = grp.index
                    vq = v[:, :, q * BANK:(q + 1) * BANK]
                    if q == 0:
                        dve.wait_ge(sgu_landed, 48)
                    dve.wait_ge(pe_done, grp.end())
                    dve.tensor_tensor(vq, banks3(g, 0, 4), many(tiles(h_f32, V_BIAS + q), 4), ALU.add)\
                       .then_inc(vsum_ready, 1)
                    if q == 0:
                        dve.wait_ge(ws_t_done, 1)
                        own.add(dve.tensor_copy(tiles(h_f32, W_T, 2), bank(s.table_g, 0, 2)))
                        own.settle()
                        later = tiles(h_f32, W_T, 2).rearrange("p (h t) -> p h t", h=SGU_HEADS)[CHUNK:P, :, 0:CHUNK]
                        dve.memset(later, 0.0).then_inc(ws_t_ready, 1)
                    if q == 1:
                        dve.wait_ge(rowsum_done, 1)
                        dve.tensor_scalar(tiles(h_f32, ROW_SUM, 2), bank(s.table_g, 2, 2), float(D_MODEL), None,
                                          ALU.mult).then_inc(rowsum_saved, 1)
                        dve.wait_ge(rowsum_saved, 1)
                    dve.wait_ge(gelu_v, q + 1)
                    for t in range(TT):
                        own.add(dve.bn_stats(small[:, t * 24 + q * 6:t * 24 + q * 6 + 6], v[:, t, q * BANK:(q + 1) * BANK]))
                    if q == 3:
                        sgu_norm()
                if s.kind == "sgu_u" and grp.index == 3:
                    sgu_gate(s)
                if s.kind in ("mixer_out", "ffn_out"):
                    residual_norm(s, grp)
                if s.kind == "ple_proj" and grp.index == 1:
                    sq = PROJ_SQ
                    dve.wait_ge(proj_sq, 2 * s.layer + 2)
                    own.add(dve.tensor_tensor(tiles(h_f32, sq, 4), tiles(h_f32, sq, 4), tiles(h_f32, sq + 4, 4), ALU.add))
                    own.settle()
                    own.add(dve.tensor_tensor(tiles(h_f32, sq, 2), tiles(h_f32, sq, 2), tiles(h_f32, sq + 2, 2), ALU.add))
                    own.settle()
                    dve.tensor_tensor(tiles(h_f32, sq), tiles(h_f32, sq), tiles(h_f32, sq + 1), ALU.add).then_inc(rms_sums, 1)
                if s.kind == "ple_gate":
                    if grp.index == 0:
                        dve.wait_ge(rms_done, s.layer + 1)
                        dve.tensor_scalar(var[:, :], bank(g + 1, 0), EPS, None, ALU.add).then_inc(rms_var, 1)
                        dve.wait_ge(rms_std, s.layer + 1)
                        own.add(dve.reciprocal(rstd[:, :], var[:, :]))
                        own.settle()
                        pr = three(tiles(h_f32, PROJ, DT), DT)
                        own.add(dve.tensor_tensor(pr, pr, many(rstd[:, :], DT), ALU.mult))
                        own.settle()
                    for j in range(TILES + 1):
                        m = TILES * grp.index + j
                        if j < TILES:
                            dve.wait_ge(gate_ready, s.gate0 + 2 * grp.index + j // 2 + 1)
                            own.add(dve.scalar_tensor_tensor(tiles(tmp, j), tiles(h_f32, PROJ + m),
                                                             col("ple_norm_g", s.layer, m), tiles(tmp, j),
                                                             ALU.mult, ALU.mult))
                            own.settle()
                            dve.tensor_tensor(tiles(xf, m), tiles(xf, m), tiles(tmp, j), ALU.add).then_inc(upd_ready, 1)
                        if j >= 1 and s.layer < DEPTH - 1:
                            lo_of(x_hi_ready, s.out0 + m, tiles(h_lo, m - 1), tiles(xf, m - 1), tiles(h_hi, m - 1))

            def sgu_norm():
                own.settle()
                mv = small[:, 96:104].rearrange("p (t c) -> p t c", t=TT)
                for t in range(TT):
                    own.add(dve.bn_aggr(small[:, 96 + 2 * t:98 + 2 * t], small[:, t * 24:(t + 1) * 24]))
                own.settle()
                dve.tensor_scalar(small[:, 104:108], mv[:, :, 1], EPS, None, ALU.add).then_inc(vvar_ready, 1)
                dve.wait_ge(vstd_ready, 1)
                own.add(dve.reciprocal(small[:, 108:112], small[:, 104:108]))
                own.settle()
                own.add(dve.scalar_tensor_tensor(small[:, 112:116], mv[:, :, 0], -1.0, small[:, 108:112],
                                                 ALU.mult, ALU.mult))
                own.settle()
                for t in range(TT):
                    dve.tensor_scalar(v[:, t, :], v[:, t, :], small[:, 108 + t:109 + t], small[:, 112 + t:113 + t],
                                      ALU.mult, ALU.add).then_inc(v_ready, 1)
                for f in range(ET):
                    head = f * P // (SGU_WIDTH // SGU_HEADS)
                    own.add(dve.scalar_tensor_tensor(
                        shift_of(f), tiles(h_f32, ROW_SUM, 2)[:, head * P:(head + 1) * P], col("b_ln_b", f // DT, f % DT),
                        tiles(h_f32, B_S, 2)[:, head * P:(head + 1) * P], ALU.mult, ALU.add))

            def shift_of(f):
                return tiles(h_f32, V_BIAS, 4)[:, f * P:(f + 1) * P]

            def sgu_gate(s):
                dve.wait_ge(gelu_u, 4)
                own.settle()
                for f in range(ET + 1):
                    if f < ET:
                        g = s.mix_g + f // TILES
                        dve.wait_ge(mix_done, f + 1)
                        uf = tiles(tmp, 4 + f % 2)
                        if f >= 2:
                            dve.wait_ge(x_ready, s.out0 + f - 1)
                        own.add(dve.scalar_tensor_tensor(
                            uf.rearrange("p (t c) -> p t c", t=TT), bank(g, f % TILES).rearrange("p (t c) -> p t c", t=TT),
                            col("b_ln_g", f // DT, f % DT), many(shift_of(f), TT), ALU.mult, ALU.add))
                        own.settle()
                        dve.tensor_tensor(uf, uf, tiles(h_f32, u_tile(f)[0]), ALU.mult).then_inc(uf_ready, 1)
                        dve.wait_ge(uf_ready, f + 1)
                    if f >= 1:
                        _, low, m = u_tile(f - 1)
                        hi = tiles(h_hi, f - 1) if f - 1 < DT else tiles(h_lo, f - 1 - DT)
                        lo_of(x_hi_ready, s.out0 + f, tiles(low, m), tiles(tmp, 4 + (f - 1) % 2), hi)

            for s in stages:
                if s.kind != "ffn_in":
                    for grp in s.groups:
                        epilogue(s, grp)
                    continue
                first, total = s.groups[0], len(s.groups)
                ffn_in_epilogue(first, first.mark, (s.gate0 + 1, total * s.layer + 1), slice(0, 2 * SEQ))
                with dve.Fori(0, (total - 1) // 2) as it:
                    for grp in s.groups[1:3]:
                        ffn_in_epilogue(grp, it * (2 * (grp.units - 1 + TILES)) + grp.mark,
                                        (it * 2 + (s.gate0 + grp.index + 1), it * 2 + (total * s.layer + grp.index + 1)),
                                        bass.ds(it * (4 * SEQ) + grp.index * 2 * SEQ, 2 * SEQ),
                                        it * 2 + (total * s.layer + grp.index))


_INS = ["x", "p", "a_w_pw1", "a_b_pw1", "a_w_dw", "a_b_dw", "a_ln_g", "a_ln_b", "a_w_pw2",
        "b_w_in", "b_b_in", "b_ln_g", "b_ln_b", "b_w_s", "b_b_s", "b_w_out",
        "c_w_in", "c_w_conv", "c_w_out", "ln1_g", "ln1_b", "ln2_g", "ln2_b",
        "ffn_w_gate", "ffn_w_up", "ffn_w_down", "ple_w_gate", "ple_w_proj", "ple_norm_g"]


def kernel(**inputs):
    import numpy as _np
    import concourse.bacc as _bacc
    from concourse.bass_utils import run_bass_kernel_spmd as _run

    nc = _bacc.Bacc("TRN2", target_bir_lowering=False, num_devices=1)
    arrays, ins = {}, {}
    for name in _INS:
        a = _np.ascontiguousarray(inputs[name])
        arrays[f"in_{name}_dram"] = a
        ins[name] = nc.dram_tensor(f"in_{name}_dram", a.shape, mybir.dt.from_np(a.dtype), kind="ExternalInput").ap()
    out = nc.dram_tensor("out_0_dram", (1, SEQ, D_MODEL), F32, kind="ExternalOutput").ap()
    trunk(nc, ins, out)
    r = _run(nc, [arrays], core_ids=[0])
    return r.results[0]["out_0_dram"]
```
